# Optimizing a Trainium2 kernel written in Bass

```python
import math
import jax, jax.numpy as jnp
from jax import lax
import numpy as np

D_MODEL = 1024
BATCH = 1
SEQ = 256
DEPTH = 2

CHUNK = 64
Q_BLOCK = 128
HEAD_DIM = 64
FOX_HEADS = D_MODEL // (2 * HEAD_DIM)
FOX_WIDTH = FOX_HEADS * HEAD_DIM
DIFF_HEADS = D_MODEL // (4 * HEAD_DIM)
DIFF_V_DIM = 2 * HEAD_DIM
DIFF_QK_WIDTH = DIFF_HEADS * 2 * HEAD_DIM
DIFF_OUT = DIFF_HEADS * DIFF_V_DIM
SWA_Q_HEADS = D_MODEL // (2 * HEAD_DIM)
SWA_KV_HEADS = 2
SWA_GROUP = SWA_Q_HEADS // SWA_KV_HEADS
SWA_WINDOW = 128
SWA_CHUNKS = SWA_WINDOW // CHUNK
SWA_Q_WIDTH = SWA_Q_HEADS * HEAD_DIM
SWA_KV_WIDTH = SWA_KV_HEADS * HEAD_DIM
CHK_HEADS = D_MODEL // (2 * HEAD_DIM)
CHK_WIDTH = CHK_HEADS * HEAD_DIM
CHK_LEFT = 8
CHK_BAND = (CHK_LEFT + 1) * CHUNK
CHK_REL_CLIP = 256
EVEN_WIDTHS = (FOX_WIDTH, FOX_WIDTH, FOX_WIDTH, FOX_HEADS, DIFF_QK_WIDTH, DIFF_QK_WIDTH, DIFF_OUT)
EVEN_IN = 3 * FOX_WIDTH + FOX_HEADS + 2 * DIFF_QK_WIDTH + DIFF_OUT
EVEN_OUT = FOX_WIDTH + DIFF_OUT
ODD_WIDTHS = (SWA_Q_WIDTH, SWA_KV_WIDTH, SWA_KV_WIDTH, CHK_WIDTH, CHK_WIDTH, CHK_WIDTH)
ODD_IN = SWA_Q_WIDTH + 2 * SWA_KV_WIDTH + 3 * CHK_WIDTH
ODD_OUT = SWA_Q_WIDTH + CHK_WIDTH
T5_BUCKETS = 32
T5_MAX_DIST = 512
T5_HEADS = SWA_Q_HEADS
PEER_HEADS = 8
PEER_NKEYS = 128
PEER_EXPERTS = PEER_NKEYS * PEER_NKEYS
PEER_TOPK = 16
PEER_DQ = 256
PEER_TOK_BLOCK = 128

NORM_EPS = 1e-6
NEG_INF = -1e30

kernel_name = 'hybrid_chunk_causal_fox_diff_swa_chunked_peer'

def rmsnorm(x, g):
    xf = x.astype(jnp.float32)
    y = xf * lax.rsqrt(jnp.mean(xf * xf, axis=-1, keepdims=True) + NORM_EPS)
    return (y * g.astype(jnp.float32)).astype(x.dtype)

def split_cols(a, widths):
    outs, start = [], 0
    for w in widths:
        outs.append(a[..., start:start + w])
        start += w
    return outs

def t5_bucket(rel):
    nb = T5_BUCKETS // 2
    max_exact = nb // 2
    ret = jnp.where(rel > 0, nb, 0)
    n = jnp.abs(rel)
    nf = jnp.maximum(n, 1).astype(jnp.float32)
    large = max_exact + (jnp.log(nf / max_exact) / math.log(T5_MAX_DIST / max_exact)
                         * (nb - max_exact)).astype(jnp.int32)
    large = jnp.minimum(large, nb - 1)
    return ret + jnp.where(n < max_exact, n, large)

def even_mixer(h, w_in, w_out, f_bias, lam_vecs, subln_g, t5_table, layer_idx):
    b, s, _ = h.shape
    nqb = s // Q_BLOCK
    f32 = jnp.float32
    proj = jnp.einsum('bsd,de->bse', h, w_in)
    fq, fk, fv, fg, dq, dk, dv = split_cols(proj, EVEN_WIDTHS)
    fq = fq.reshape(b, s, FOX_HEADS, HEAD_DIM)
    fk = fk.reshape(b, s, FOX_HEADS, HEAD_DIM)
    fv = fv.reshape(b, s, FOX_HEADS, HEAD_DIM)
    log_f = jax.nn.log_sigmoid(fg.astype(f32) + f_bias.astype(f32))
    cum_f = jnp.cumsum(log_f, axis=1)
    cum_fk = cum_f.transpose(0, 2, 1)
    dq = dq.reshape(b, s, DIFF_HEADS, 2, HEAD_DIM)
    dk = dk.reshape(b, s, DIFF_HEADS, 2, HEAD_DIM)
    dv = dv.reshape(b, s, DIFF_HEADS, DIFF_V_DIM)
    lv = lam_vecs.astype(f32)
    lam_init = 0.8 - 0.6 * math.exp(-0.3 * layer_idx)
    lam = jnp.exp(jnp.sum(lv[0] * lv[1])) - jnp.exp(jnp.sum(lv[2] * lv[3])) + lam_init
    kpos = jnp.arange(s)
    kchunk = kpos // CHUNK
    t5_d = t5_table[:, :DIFF_HEADS].T.astype(f32)
    scale = HEAD_DIM ** -0.5

    def to_blocks(a):
        return jnp.moveaxis(a.reshape((b, nqb, Q_BLOCK) + a.shape[2:]), 1, 0)

    def block(args):
        fq_i, cf_i, dq_i, qpos = args
        sf = jnp.einsum('bqhd,bkhd->bhqk', fq_i, fk, preferred_element_type=f32) * scale
        sf = sf + cf_i.transpose(0, 2, 1)[..., None] - cum_fk[:, :, None, :]
        sf = jnp.where(kpos[None, :] <= qpos[:, None], sf, NEG_INF)
        pf = jax.nn.softmax(sf, axis=-1).astype(fv.dtype)
        of = jnp.einsum('bhqk,bkhd->bqhd', pf, fv)
        sd = jnp.einsum('bqhmd,bkhmd->bhmqk', dq_i, dk, preferred_element_type=f32) * scale
        sd = sd + t5_d[:, t5_bucket(kpos[None, :] - qpos[:, None])][None, :, None]
        sd = jnp.where(kchunk[None, :] <= (qpos // CHUNK)[:, None], sd, NEG_INF)
        pd = jax.nn.softmax(sd, axis=-1)
        pd = (pd[:, :, 0] - lam * pd[:, :, 1]).astype(dv.dtype)
        od = jnp.einsum('bhqk,bkhe->bqhe', pd, dv)
        od = rmsnorm(od, subln_g) * (1.0 - lam_init)
        return (of.reshape(b, Q_BLOCK, FOX_WIDTH), od.reshape(b, Q_BLOCK, DIFF_OUT).astype(of.dtype))

    qpos_blocks = kpos.reshape(nqb, Q_BLOCK)
    of, od = lax.map(block, (to_blocks(fq), to_blocks(cum_f), to_blocks(dq), qpos_blocks))
    of = jnp.moveaxis(of, 0, 1).reshape(b, s, FOX_WIDTH)
    od = jnp.moveaxis(od, 0, 1).reshape(b, s, DIFF_OUT)
    return jnp.einsum('bse,ed->bsd', jnp.concatenate([of, od], axis=-1), w_out)

def odd_mixer(h, w_in, w_out, sinks, rel_table, t5_table):
    b, s, _ = h.shape
    nc = s // CHUNK
    f32 = jnp.float32
    proj = jnp.einsum('bsd,de->bse', h, w_in)
    sq, sk, sv, cq, ck, cv = split_cols(proj, ODD_WIDTHS)
    scale = HEAD_DIM ** -0.5
    ci = jnp.arange(CHUNK)

    band = SWA_CHUNKS * CHUNK
    q = sq.reshape(b, nc, CHUNK, SWA_KV_HEADS, SWA_GROUP, HEAD_DIM)

    def band_gather(a):
        ap = jnp.pad(a, ((0, 0), ((SWA_CHUNKS - 1) * CHUNK, 0), (0, 0), (0, 0)))
        ap = ap.reshape(b, nc + SWA_CHUNKS - 1, CHUNK, SWA_KV_HEADS, HEAD_DIM)
        return jnp.concatenate([ap[:, j:j + nc] for j in range(SWA_CHUNKS)], axis=2)

    kb = band_gather(sk.reshape(b, s, SWA_KV_HEADS, HEAD_DIM))
    vb = band_gather(sv.reshape(b, s, SWA_KV_HEADS, HEAD_DIM))
    jpos = jnp.arange(band)
    rel = jpos[None, :] - (SWA_CHUNKS - 1) * CHUNK - ci[:, None]
    t5b = t5_table.astype(f32)[t5_bucket(rel)].transpose(2, 0, 1).reshape(SWA_KV_HEADS, SWA_GROUP, CHUNK, band)
    valid = (jnp.arange(nc)[:, None] * CHUNK - (SWA_CHUNKS - 1) * CHUNK + jpos[None, :]) >= 0
    sc = jnp.einsum('bcikgd,bcjkd->bkgcij', q, kb, preferred_element_type=f32) * scale
    sc = sc + t5b[:, :, None]
    sc = jnp.where(valid[:, None, :], sc, NEG_INF)
    sink = sinks.astype(f32).reshape(SWA_KV_HEADS, SWA_GROUP)[None, :, :, None, None, None]
    m = jnp.maximum(jnp.max(sc, axis=-1, keepdims=True), sink)
    e = jnp.exp(sc - m)
    p = e / (jnp.sum(e, axis=-1, keepdims=True) + jnp.exp(sink - m))
    oc = jnp.einsum('bkgcij,bcjkd->bcikgd', p.astype(sv.dtype), vb).reshape(b, s, SWA_Q_WIDTH)

    qd = jnp.moveaxis(cq.reshape(b, nc, CHUNK, CHK_HEADS, HEAD_DIM), 1, 0)
    pad = CHK_LEFT * CHUNK
    kp = jnp.pad(ck.reshape(b, s, CHK_HEADS, HEAD_DIM), ((0, 0), (pad, 0), (0, 0), (0, 0)))
    vp = jnp.pad(cv.reshape(b, s, CHK_HEADS, HEAD_DIM), ((0, 0), (pad, 0), (0, 0), (0, 0)))
    jb = jnp.arange(CHK_BAND)
    rel_d = pad + ci[:, None] - jb[None, :]
    bias_d = rel_table.astype(f32)[jnp.clip(rel_d, -CHK_REL_CLIP, CHK_REL_CLIP) + CHK_REL_CLIP].transpose(2, 0, 1)

    def chunk_step(args):
        q_c, c_idx = args
        k_c = lax.dynamic_slice_in_dim(kp, c_idx * CHUNK, CHK_BAND, axis=1)
        v_c = lax.dynamic_slice_in_dim(vp, c_idx * CHUNK, CHK_BAND, axis=1)
        s_c = jnp.einsum('bihd,bjhd->bhij', q_c, k_c, preferred_element_type=f32) * scale + bias_d
        s_c = jnp.where((c_idx * CHUNK - pad + jb) >= 0, s_c, NEG_INF)
        p_c = jax.nn.softmax(s_c, axis=-1).astype(v_c.dtype)
        return jnp.einsum('bhij,bjhd->bihd', p_c, v_c).reshape(b, CHUNK, CHK_WIDTH)

    od = lax.map(chunk_step, (qd, jnp.arange(nc)))
    od = jnp.moveaxis(od, 0, 1).reshape(b, s, CHK_WIDTH)
    return jnp.einsum('bse,ed->bsd', jnp.concatenate([oc, od], axis=-1), w_out)

def peer(h, w_q, sub_keys, u_tab, v_tab):
    b, s, d = h.shape
    t = b * s
    f32 = jnp.float32
    xt = h.reshape(t, d)
    q = jnp.einsum('td,de->te', xt, w_q).reshape(t, PEER_HEADS, 2, PEER_DQ // 2)
    sc = jnp.einsum('thpd,hpnd->thpn', q, sub_keys, preferred_element_type=f32)
    v1, i1 = lax.top_k(sc[:, :, 0], PEER_TOPK)
    v2, i2 = lax.top_k(sc[:, :, 1], PEER_TOPK)
    cand = (v1[..., :, None] + v2[..., None, :]).reshape(t, PEER_HEADS, PEER_TOPK * PEER_TOPK)
    cand_idx = (i1[..., :, None] * PEER_NKEYS + i2[..., None, :]).reshape(t, PEER_HEADS, PEER_TOPK * PEER_TOPK)
    top_v, top_pos = lax.top_k(cand, PEER_TOPK)
    eidx = jnp.take_along_axis(cand_idx, top_pos, axis=-1)
    gates = jax.nn.softmax(top_v, axis=-1)
    nb = t // PEER_TOK_BLOCK
    hk = PEER_HEADS * PEER_TOPK

    def blk(args):
        xb, ib, gb = args
        a = jnp.einsum('tkd,td->tk', u_tab[ib], xb, preferred_element_type=f32)
        a = jax.nn.gelu(a, approximate=False) * gb
        return jnp.einsum('tk,tkd->td', a.astype(xb.dtype), v_tab[ib])

    out = lax.map(blk, (xt.reshape(nb, PEER_TOK_BLOCK, d),
                        eidx.reshape(nb, PEER_TOK_BLOCK, hk),
                        gates.reshape(nb, PEER_TOK_BLOCK, hk)))
    return out.reshape(b, s, d)

def setup_inputs(seed: int = 0) -> dict:
    key = jax.random.key(seed)
    ks = jax.random.split(key, 24)
    n_even = (DEPTH + 1) // 2
    n_odd = DEPTH // 2
    f32 = jnp.float32

    def nrm(k, shape, sc):
        return jax.random.normal(k, shape, f32) * sc

    inv = D_MODEL ** -0.5
    return {
        'x': nrm(ks[0], (BATCH, SEQ, D_MODEL), 1.0),
        'c': nrm(ks[1], (BATCH, D_MODEL), 1.0),
        't5_bias': nrm(ks[2], (T5_BUCKETS, T5_HEADS), 0.5),
        'norm_mix': 1.0 + nrm(ks[3], (DEPTH, D_MODEL), 0.05),
        'norm_ffn': 1.0 + nrm(ks[4], (DEPTH, D_MODEL), 0.05),
        'w_mod': nrm(ks[5], (DEPTH, D_MODEL, 6 * D_MODEL), 0.5 * inv),
        'b_mod': nrm(ks[6], (DEPTH, 6 * D_MODEL), 0.02),
        'even_w_in': nrm(ks[7], (n_even, D_MODEL, EVEN_IN), inv),
        'even_w_out': nrm(ks[8], (n_even, EVEN_OUT, D_MODEL), EVEN_OUT ** -0.5),
        'fox_f_bias': 3.0 + nrm(ks[9], (n_even, FOX_HEADS), 0.5),
        'diff_lambda': nrm(ks[10], (n_even, 4, HEAD_DIM), 0.1),
        'diff_subln': 1.0 + nrm(ks[11], (n_even, DIFF_V_DIM), 0.05),
        'odd_w_in': nrm(ks[12], (n_odd, D_MODEL, ODD_IN), inv),
        'odd_w_out': nrm(ks[13], (n_odd, ODD_OUT, D_MODEL), ODD_OUT ** -0.5),
        'swa_sinks': nrm(ks[14], (n_odd, SWA_Q_HEADS), 0.5),
        'chunk_rel_bias': nrm(ks[15], (n_odd, 2 * CHK_REL_CLIP + 1, CHK_HEADS), 0.5),
        'peer_w_q': nrm(ks[16], (DEPTH, D_MODEL, PEER_HEADS * PEER_DQ), inv),
        'peer_sub_keys': nrm(ks[17], (DEPTH, PEER_HEADS, 2, PEER_NKEYS, PEER_DQ // 2), (PEER_DQ // 2) ** -0.5),
        'peer_u': nrm(ks[18], (DEPTH, PEER_EXPERTS, D_MODEL), inv),
        'peer_v': nrm(ks[19], (DEPTH, PEER_EXPERTS, D_MODEL), 0.25),
        'final_norm': 1.0 + nrm(ks[20], (D_MODEL,), 0.05),
    }

def reference(x, c, t5_bias, norm_mix, norm_ffn, w_mod, b_mod,
              even_w_in, even_w_out, fox_f_bias, diff_lambda, diff_subln,
              odd_w_in, odd_w_out, swa_sinks, chunk_rel_bias,
              peer_w_q, peer_sub_keys, peer_u, peer_v, final_norm):
    cs = jax.nn.silu(c)
    for l in range(DEPTH):
        mod = jnp.einsum('bd,de->be', cs, w_mod[l]) + b_mod[l]
        sh1, sc1, g1, sh2, sc2, g2 = jnp.split(mod, 6, axis=-1)
        h = rmsnorm(x, norm_mix[l]) * (1.0 + sc1[:, None]) + sh1[:, None]
        j = l // 2
        if l % 2 == 0:
            y = even_mixer(h, even_w_in[j], even_w_out[j], fox_f_bias[j], diff_lambda[j],
                           diff_subln[j], t5_bias, l)
        else:
            y = odd_mixer(h, odd_w_in[j], odd_w_out[j], swa_sinks[j], chunk_rel_bias[j], t5_bias)
        x = x + g1[:, None] * y
        h = rmsnorm(x, norm_ffn[l]) * (1.0 + sc2[:, None]) + sh2[:, None]
        x = x + g2[:, None] * peer(h, peer_w_q[l], peer_sub_keys[l], peer_u[l], peer_v[l])
    return rmsnorm(x, final_norm)


_drawn_inputs = setup_inputs


def setup_inputs(seed=0):
    import zlib

    import numpy as np

    out = dict(_drawn_inputs(seed))
    spreads = {}
    factors = {'norm_mix': 4.233,
     'norm_ffn': 4.187,
     'diff_lambda': 3.19,
     'diff_subln': 5.349,
     'swa_sinks': 64.0,
     'chunk_rel_bias': 3.287}
    for name, (base, spread) in spreads.items():
        noise = np.random.default_rng([zlib.crc32(name.encode()), seed]).standard_normal(out[name].shape)
        drawn = base * np.exp(spread * noise) if base else spread * noise
        out[name] = __import__('jax').numpy.asarray(drawn.astype(out[name].dtype))
    for name, factor in factors.items():
        out[name] = (out[name] * factor).astype(out[name].dtype)
    return out
```

```python
import math
from contextlib import ExitStack

import numpy as np

import concourse.bass as bass
from concourse import mybir

ALU = mybir.AluOpType
ACT = mybir.ActivationFunctionType
F32 = mybir.dt.float32
F32R = mybir.dt.float32r
U32 = mybir.dt.uint32
BF16 = mybir.dt.bfloat16
AX_X = mybir.AxisListType.X

P = 128
D = 1024
KT = D // P
T = 256
TT = T // P
LAYERS = 2
HD = 64
CHUNK = 64
MAPS = 16
MAPW = 3 * P
PH = 8
TOPK = 16
NKEY = 128
NMOD = 6 * KT
NEG = -1e30
EPS = 1e-6
LAM_INIT = 0.8 - 0.6 * math.exp(-0.3 * 0)
RINGS = 2
MODS = 3
EARLY = 2 * KT
WQ_RING = 4
WIDE = 4
NCAND = WIDE * TOPK + (TOPK - WIDE) * 4
HALF = D // 2

QK_TILES = (16, 13)
V_WIDTHS = ((512, 512), (512, 128))
Q_TILES = (tuple(range(0, 4)) + tuple(range(8, 12)), tuple(range(0, 4)) + tuple(range(5, 9)))
GATE_COLS = 8

C_ID, C_ONE, C_IOTA = 0, P, 2 * P
C_END = 3 * P


def win_cols(l):
    return QK_TILES[l] * KT * P + sum(V_WIDTHS[l]) * KT + (GATE_COLS * KT if l == 0 else 0)


QK_AT = win_cols(0)
V_AT = QK_AT + 16 * T
BIAS_AT = (V_AT + TT * D, win_cols(1))
S_AT = 0
PT_AT = MAPS * MAPW
WOUT_AT = PT_AT + 4 * MAPW
WQ_AT = WOUT_AT + KT * D
QS_AT = QK_AT
KEYS_AT = QS_AT + 2 * 2 * T
OUT_AT = KEYS_AT
BIG = P * T

Q_VAL, Q_IDX, Q_TOP, Q_POS, Q_REP, Q_CAND, Q_REP2 = 0, 512, 1024, 1280, 1536, 2048, 2560
Q_TMP, Q_IDF, Q_A, Q_B, Q_AF, Q_BF, Q_E, Q_G = 3072, 5120, 5632, 5888, 6144, 6400, 7168, 7424
Q_KEY = WOUT_AT
Q_HOT = WQ_AT


def attention_maps(l):
    out = []
    for i in range(MAPS):
        half = (i % 2) * HD
        if l == 0:
            out.append((i // 2, 4 + i // 2, half, 0) if i < 8 else (8 + (i - 8) // 2, 12 + (i - 8) // 2, half, 1 + (i - 8) // 2))
        else:
            out.append((i // 2, 4, half, i) if i < 8 else (5 + (i - 8) // 2, 9 + (i - 8) // 2, half, i))
    return out


def value_products(l):
    out = []
    if l == 0:
        out += [(i, i * HD, HD, i // 2, (i % 2) * HD) for i in range(8)]
        out += [(8 + 2 * h, 512 + h * 2 * HD, 2 * HD, 4 + h, 0) for h in range(4)]
    else:
        out += [(i, 512 + (i % 2) * HD, HD, i // 2, (i % 2) * HD) for i in range(8)]
        out += [(8 + h, h * HD, HD, 4 + h // 2, (h % 2) * HD) for h in range(8)]
    return out


def build(nc, a, out):
    with ExitStack() as ctx:
        def sb(name, shape, dt=F32):
            return ctx.enter_context(nc.sbuf_tensor(name, shape, dt))

        def sem(name):
            return ctx.enter_context(nc.semaphore(name))

        big = sb("big", [P, BIG])
        raw = sb("raw", [P, 2 * RINGS, D])
        xT = raw[:, 0:2].rearrange("p a (k t) -> p (a k) t", t=T)
        hT = raw[:, 2:4].rearrange("p a (k t) -> p (a k) t", t=T)
        x_hi = sb("x_hi", [P, KT, T], F32R)
        x_lo = sb("x_lo", [P, KT, T], F32R)
        u_hi = sb("u_hi", [P, D], F32R)
        u_lo = sb("u_lo", [P, D], F32R)
        v_hi = sb("v_hi", [P, D], F32R)
        v_lo = sb("v_lo", [P, D], F32R)
        a_hi = sb("a_hi", [P, 2, T], F32R)
        a_lo = sb("a_lo", [P, 2, T], F32R)
        wmod_ring = sb("wmod_ring", [P, MODS, D])
        cst = sb("cst", [P, C_END])
        par = sb("par", [P, 640])
        c_all = sb("c_all", [P, D])
        work = sb("work", [P, 4, T])
        stat = sb("stat", [P, 256])
        pick = wmod_ring[:, 2, 0:3 * T].rearrange("p (a t) -> p a t", a=3)
        hot = [x.rearrange("p (a t n) -> p a t n", a=2, n=P) for x in (wmod_ring[:, 0], wmod_ring[:, 1], raw[:, 2], raw[:, 3])]
        hot_bf = [x.bitcast(BF16).rearrange("p (n t) -> p n t", t=4) for x in (work[:, 2], work[:, 3])]
        iota_bf = wmod_ring[:, 2, 3 * T:].bitcast(BF16).rearrange("p (n t) -> p n t", t=4)
        pick_bf = work[:, 1].bitcast(BF16)[:, 0:T]
        bank = [ctx.enter_context(nc.psum_tensor(f"bank{i}", [P, 512], F32)) for i in range(8)]

        ident = cst[:, C_ID:C_ID + P]
        ones = cst[:, C_ONE:C_ONE + P]
        iota = cst[:, C_IOTA:C_IOTA + P]

        def selector(h):
            return ident[0:8, h:h + 1].to_broadcast([8, P])

        def b_mod(l):
            return par[:, l * NMOD:(l + 1) * NMOD]

        def gain(n):
            return par[:, 96 + n * KT:96 + (n + 1) * KT]

        f_bias = par[0:8, 136:137]
        subln = par[:, 137:138]
        sinks = par[:, 144:152]
        lam_in = par[:, 152:408].rearrange("p (a b) -> p a b", a=4)
        mod = [par[:, 408 + l * NMOD:408 + (l + 1) * NMOD] for l in range(LAYERS)]
        amp = [[par[:, 504 + (2 * l + n) * KT:504 + (2 * l + n + 1) * KT] for n in range(2)] for l in range(LAYERS)]
        lam = par[:, 536:544]
        subln_s = par[:, 544:545]

        mx = stat[:, 0:32]
        neg = stat[:, 32:64]
        den = stat[:, 64:96]
        rec = stat[:, 96:128]
        snk = stat[:, 128:160]
        gsum = stat[:, 160:176]
        grec = stat[:, 176:192]
        tile_sum = stat[:, 192:194]

        scores = big[:, S_AT:S_AT + MAPS * MAPW].rearrange("p (m n) -> p m n", m=MAPS)
        pT = big[:, PT_AT:PT_AT + 4 * MAPW].rearrange("p (m n) -> p m n", m=4)
        qk = big[:, QK_AT:QK_AT + 16 * T].rearrange("p (m n) -> p m n", m=16)
        vv = big[:, V_AT:V_AT + TT * D].rearrange("p (m n) -> p m n", m=TT)
        wq = big[:, WQ_AT:WQ_AT + WQ_RING * 2 * D].rearrange("p (h s k n) -> p h s k n", h=WQ_RING, s=2, k=KT)
        qs = big[:, QS_AT:QS_AT + 4 * T].rearrange("p (r s n) -> p r s n", r=2, s=2)
        keys = big[:, KEYS_AT:KEYS_AT + PH * 2 * NKEY].rearrange("p (h s n) -> p h s n", h=PH, s=2)
        wout = big[:, WOUT_AT:WOUT_AT + KT * D].rearrange("p (m k n) -> p m k n", m=KT, k=KT)
        x_store = nc.dram_tensor("x_store", (P, KT * T), F32, kind="Internal").ap()
        gates = big[:].rearrange("p (j t) -> p j t", j=NKEY)
        yt = big[:, OUT_AT:OUT_AT + TT * D].rearrange("p (t n) -> p t n", t=TT)
        cum, negcum, softp, minz = (work[0:8, n, :] for n in range(4))

        def bias_map(l, n):
            return big[:, BIAS_AT[l] + n * MAPW:BIAS_AT[l] + (n + 1) * MAPW]

        def w_qk(l, m, k):
            return big[:, (m * KT + k) * P:(m * KT + k + 1) * P]

        def w_v(l, part, k):
            at = QK_TILES[l] * D + (V_WIDTHS[l][0] * KT if part else 0) + k * V_WIDTHS[l][part]
            return big[:, at:at + V_WIDTHS[l][part]]

        def w_gate(k):
            at = QK_TILES[0] * D + sum(V_WIDTHS[0]) * KT + k * GATE_COLS
            return big[:, at:at + GATE_COLS]

        def q_area(at, size, **kw):
            names = list(kw)
            v = big[:, at:at + size]
            return v.rearrange("p (" + " ".join(names) + ") -> p " + " ".join(names), **{k: kw[k] for k in names[:-1]}) if names else v

        q_val = q_area(Q_VAL, 512, t=TT, h=PH, s=2, k=TOPK)
        q_idx = q_area(Q_IDX, 512, t=TT, h=PH, s=2, k=TOPK).bitcast(U32)
        q_top = q_area(Q_TOP, 256, t=TT, h=PH, k=TOPK)
        q_pos = q_area(Q_POS, 256, t=TT, h=PH, k=TOPK).bitcast(U32)
        q_rep = q_area(Q_REP, 512, s=2, t=TT, n=NKEY)
        q_cand = q_area(Q_CAND, TT * NCAND, t=TT, n=NCAND)
        q_rep2 = q_area(Q_REP2, TT * NCAND, t=TT, n=NCAND)
        q_key = q_area(Q_KEY, 1024, r=2, s=2, t=TT, n=NKEY)
        q_hot = [q_area(Q_HOT + 2048 * n, 2048, h=PH, k=TOPK, a=TOPK) for n in range(4)]
        q_idf = q_area(Q_IDF, 512, t=TT, h=PH, s=2, k=TOPK)
        q_ab = [q_area(at, 256).bitcast(U32) for at in (Q_A, Q_B, Q_TMP, Q_TMP + 256)]
        q_tmp = [q_area(Q_TMP + 256 * n, 256) for n in (2, 3, 4)]
        q_abf = [q_area(Q_AF, 256, t=TT, n=P), q_area(Q_BF, 256, t=TT, n=P)]
        q_e = q_area(Q_E, 256, t=TT, h=PH, k=TOPK)
        q_g = q_area(Q_G, 256, t=TT, h=PH, k=TOPK)

        const_in = sem("const_in")
        c_in = sem("c_in")
        out_done = sem("out_done")
        win_in = [sem(f"win_in{n}") for n in range(7)]
        bias_in = sem("bias_in")
        wout_in = sem("wout_in")
        wq_in = [sem(f"wq_in{n}") for n in range(WQ_RING)]
        keys_in = sem("keys_in")
        wm_in = [sem(f"wm_in{n}") for n in range(MODS)]
        wm1_in = [sem(f"wm1_in{n}") for n in range(2)]
        u_in = [sem(f"u_in{n}") for n in range(RINGS)]
        v_in = [sem(f"v_in{n}") for n in range(RINGS)]
        x_stored = sem("x_stored")
        x_back = sem("x_back")
        dve_step = sem("dve_step")
        act_step = sem("act_step")
        silu_e = sem("silu_e")
        lam_e = sem("lam_e")
        lam_s = sem("lam_s")
        names = ("mod_tile", "mod_kept", "qk_ps", "qk_act", "qk_dve", "cum_ready",
                 "map_ps", "map_max", "neg_ready", "exp_done", "prob_ready", "pt_ps", "pt_copied", "av_ps", "av_copied",
                 "sub_sq", "sub_ps", "sub_rec", "sub_root", "mix_ready", "y_ps", "x_mixed",
                 "q_ps", "q_copied", "key_ps", "key_copied", "key_free", "equal_ready", "sel_ready", "gate_max", "gate_exp", "pick_ready", "pick_ps", "pick_copied",
                 "hot_first", "hot_second", "hot_gate", "hot_used", "g_copied", "xh_done", "xl_done", "uh_done", "ul_done", "u_used",
                 "s_gelu", "a_ready", "ah_done", "al_done", "vh_done", "vl_done", "v_used",
                 "e_copied", "eT_ps", "x_done")
        s = [{n: sem(f"{n}_{l}") for n in names} for l in range(LAYERS)]
        norm_names = ("sq_ready", "ss_ps", "rec_ready", "root_ready", "hat_ready", "h_ready")
        norms = {n: sem(n) for n in norm_names}

        QK_UNITS = [QK_TILES[l] + 2 * TT + (1 if l == 0 else 0) for l in range(LAYERS)]

        def unit_counts(l):
            n = QK_UNITS[l]
            return (n + 1) // 2, n // 2

        block = ctx.enter_context(nc.Block())

        @block.sync
        def _(sp):
            sp.dma_start(c_all[:], a["c"].to_broadcast([P, D])).then_inc(c_in, 16)
            for name, dst in (("x", raw[:, 0:2].rearrange("p a n -> p (a n)")), ("consts", cst[:]), ("params", par[:, 0:408])):
                sp.dma_start(dst, a[name]).then_inc(const_in, 16)
            def load_mod(n, r):
                sp.dma_start(wmod_ring[:, r], a["w_mod"][0, n]).then_inc(wm_in[r], 16)

            for r in range(MODS):
                load_mod(r, r)
            early = -(-EARLY // MODS)
            for lo, hi in ((1, early), (early, NMOD // MODS)):
                if lo == early:
                    sp.wait_ge(s[0]["qk_ps"], 4)
                with sp.Fori(lo, hi) as i:
                    for r in range(MODS):
                        sp.wait_ge(s[0]["mod_tile"], MODS * i + r - (MODS - 1))
                        load_mod(MODS * i + r, r)
            for l in range(LAYERS):
                def load_u(j, r):
                    sp.dma_start(raw[:, r], a["u"][l, j]).then_inc(u_in[r], 16)

                def load_v(j, r):
                    sp.dma_start(raw[:, RINGS + r], a["v"][l, j]).then_inc(v_in[r], 16)

                sp.wait_ge(s[l]["x_mixed"], KT)
                sp.dma_start(x_store, raw[:, 0:2].rearrange("p a n -> p (a n)")).then_inc(x_stored, 16)
                sp.wait_ge(x_stored, 16 * (l + 1))
                sp.wait_ge(norms["hat_ready"], KT * (2 * l + 2))
                for r in range(RINGS):
                    load_u(r, r)
                sp.wait_ge(s[l]["hot_used"], T // 4)
                for r in range(RINGS):
                    load_v(r, r)
                with sp.Fori(1, NKEY // RINGS) as i:
                    for r in range(RINGS):
                        sp.wait_ge(s[l]["ul_done"], 4 * i + 2 * r - 2)
                        load_u(RINGS * i + r, r)
                        sp.wait_ge(s[l]["vl_done"], 4 * i + 2 * r - 2)
                        load_v(RINGS * i + r, r)
                sp.wait_ge(s[l]["ul_done"], 2 * NKEY)
                sp.dma_start(raw[:, 0:2].rearrange("p a n -> p (a n)"), x_store).then_inc(x_back, 16)
            sp.wait_ge(norms["hat_ready"], 5 * KT)
            sp.dma_start(out.rearrange("(k p) t -> p k t", p=P), hT[:]).then_inc(out_done, 16)
            sp.wait_ge(out_done, 16)

        @block.gpsimd
        def _(pool):
            for l in range(LAYERS):
                w = a[f"w_in{l}"]
                q4 = [(4 * D * n, min(4 * D * (n + 1), QK_TILES[l] * D)) for n in range(4)]
                at = QK_TILES[l] * D
                v0, v1 = at + KT * V_WIDTHS[l][0], at + KT * sum(V_WIDTHS[l])
                spans = q4 + [(at, v0), (v0, v1), (v1, v1 + GATE_COLS * KT)][:3 if l == 0 else 2]
                for n, (b, e) in enumerate(spans):
                    if l == 0 and n == 1:
                        pool.wait_ge(s[0]["mod_tile"], EARLY - MODS)
                    if l:
                        pool.wait_ge(s[0]["a_ready"], -(-e // T))
                    pool.dma_start(big[:, b:e], w[:, b:e]).then_inc(win_in[n], 16)
                nb = (5, MAPS)[l] * MAPW
                if l:
                    pool.wait_ge(s[0]["a_ready"], -(-(BIAS_AT[1] + nb) // T))
                pool.dma_start(big[:, BIAS_AT[l]:BIAS_AT[l] + nb], a[f"bias{l}"]).then_inc(bias_in, 16)
                pool.wait_ge(s[l]["qk_ps"], QK_UNITS[l])
                pool.dma_start(big[:, WOUT_AT:WOUT_AT + KT * D], a["w_out"][l]).then_inc(wout_in, 16)
                for h in range(PH):
                    if h == 1:
                        pool.wait_ge(s[l]["map_max"], 2 * MAPS)
                        pool.dma_start(big[:, KEYS_AT:KEYS_AT + 2 * D], a["keys"][l]).then_inc(keys_in, 16)
                    if h >= WQ_RING:
                        pool.wait_ge(s[l]["q_ps"], 2 * (h - WQ_RING) + 2)
                    at = WQ_AT + (h % WQ_RING) * 2 * D
                    pool.dma_start(big[:, at:at + 2 * D], a["w_q"][l, :, h * 2 * D:(h + 1) * 2 * D]).then_inc(wq_in[h % WQ_RING], 16)

                for n in range(4):
                    t, side = n // 2, n % 2
                    pool.wait_ge(s[l]["equal_ready"], n + 1)
                    numbers = q_idf[:, t, :, side, :].unsqueeze(2).to_broadcast([P, PH, TOPK, TOPK])
                    nc.gpsimd.tensor_tensor(q_hot[n], q_hot[n], numbers, ALU.mult).then_inc(s[l]["sel_ready"], 1)

                def weigh(g, r):
                    pool.wait_ge(s[l]["hot_second"], g + 1)
                    gate = pick[:, 2, bass.ds(4 * g, 4)].unsqueeze(2).to_broadcast([P, 4, P])
                    nc.gpsimd.tensor_tensor(hot[r][:, 1], hot_bf[r % 2].rearrange("p n t -> p t n"), gate, ALU.mult).then_inc(s[l]["hot_gate"], 1)

                with pool.Fori(0, T // 16) as i:
                    for r in range(4):
                        weigh(4 * i + r, r)
                if l == 0:
                    pool.wait_ge(s[0]["hot_used"], T // 4)
                    for r in range(2):
                        pool.dma_start(wmod_ring[:, r], a["w_mod"][1, r]).then_inc(wm1_in[r], 16)
                    with pool.Fori(1, NMOD // 2) as i:
                        for r in range(2):
                            pool.wait_ge(s[1]["mod_tile"], 2 * i + r - 1)
                            pool.dma_start(wmod_ring[:, r], a["w_mod"][1, 2 * i + r]).then_inc(wm1_in[r], 16)

        @block.tensor
        def _(pe):
            def mm(o, w, x, start=True, stop=True, free=False):
                return nc.tensor.matmul(o, w, x, start=start, stop=stop, skip_group_check=free)

            def squares(i, k):
                pe.wait_ge(norms["sq_ready"], KT * i + k + 1)
                mm(bank[7 if i % 2 else 0][:, 0:T], ones, work[:, k % 4, :], k == 0, k == KT - 1).then_inc(norms["ss_ps"], 1)

            def project(l):
                for u in range(QK_UNITS[l]):
                    if u >= 4:
                        pe.wait_ge(s[l]["qk_act" if u % 2 == 0 else "qk_dve"], (u - 4) // 2 + 1)
                    o = bank[u % 4]
                    n = u - QK_TILES[l]
                    if n < 0:
                        if u % 4 == 0:
                            pe.wait_ge(win_in[u // 4], 16 * (l + 1))
                        for k in range(KT):
                            if u == 0:
                                pe.wait_ge(norms["h_ready"], KT * 2 * l + k + 1)
                            last = mm(o[:, 0:T], w_qk(l, u, k), hT[:, k, :], k == 0, k == KT - 1)
                    elif n < 2 * TT:
                        part, t = n // TT, n % TT
                        pe.wait_ge(win_in[4 + part], 16 * (l + 1))
                        for k in range(KT):
                            last = mm(o[:, 0:V_WIDTHS[l][part]], hT[:, k, t * P:(t + 1) * P], w_v(l, part, k), k == 0, k == KT - 1)
                    else:
                        pe.wait_ge(win_in[6], 16)
                        for k in range(KT):
                            last = mm(o[0:GATE_COLS, 0:T], w_gate(k), hT[:, k, :], k == 0, k == KT - 1)
                    last.then_inc(s[l]["qk_ps"], 1)

            def map_scores(l, i):
                tq, tk, at, _ = attention_maps(l)[i]
                if i >= 4:
                    pe.wait_ge(s[l]["map_max"], 2 * (i - 3))
                o = bank[i % 4]
                fox = l == 0 and i < 8
                for t in range(TT):
                    w = P * (t + 1)
                    c = o[:, P * t:P * t + w]
                    last = mm(c, qk[at:at + HD, tq, t * P:(t + 1) * P], qk[at:at + HD, tk, 0:w], True, not fox)
                    if fox:
                        mm(c, selector(i), negcum[:, 0:w], False, False)
                        for u in range(t + 1):
                            last = mm(c[:, u * P:(u + 1) * P], cum[:, t * P:(t + 1) * P], selector(i), False, u == t)
                last.then_inc(s[l]["map_ps"], 1)

            def turn(l, n):
                i = value_products(l)[n][0]
                pe.wait_ge(s[l]["prob_ready"], i // 4 + 1)
                if n >= 2:
                    pe.wait_ge(s[l]["pt_copied"], n - 1)
                for c in range(3):
                    last = nc.tensor.transpose(bank[4 + n % 2][:, c * P:(c + 1) * P], scores[:, i, c * P:(c + 1) * P], ident)
                last.then_inc(s[l]["pt_ps"], 1)

            def values(l, n):
                _, col, w, tile, at = value_products(l)[n]
                pe.wait_ge(s[l]["pt_copied"], n + 1)
                if tile >= 2:
                    pe.wait_ge(s[l]["av_copied"], tile - 1)
                o = bank[6 + tile % 2][at:at + w, 0:T]
                mm(o, vv[:, 0, col:col + w], pT[:, n % 4, 0:T], True, False)
                last = mm(o[:, P:T], vv[:, 1, col:col + w], pT[:, n % 4, T:MAPW], False, True)
                if at + w == P:
                    last.then_inc(s[l]["av_ps"], 1)

            def attend(l):
                a_n, v_n = unit_counts(l)
                pe.wait_ge(s[l]["qk_act"], a_n)
                pe.wait_ge(s[l]["qk_dve"], v_n)
                if l == 0:
                    pe.wait_ge(s[l]["cum_ready"], 2)
                prods = value_products(l)
                done = 0
                for g in range(6):
                    if g < 4:
                        for i in range(4 * g, 4 * g + 4):
                            map_scores(l, i)
                    if g >= 2:
                        ready = [n for n, v in enumerate(prods) if v[0] < 4 * (g - 1)]
                        while done < len(ready):
                            turn(l, done)
                            if done:
                                values(l, done - 1)
                            done += 1
                values(l, done - 1)

            def mixer_out(l):
                if l == 0:
                    pe.wait_ge(s[0]["mix_ready"], 1)
                else:
                    pe.wait_ge(s[1]["av_copied"], KT)
                pe.wait_ge(wout_in, 16 * (l + 1))
                for m in range(KT):
                    if m >= 4:
                        pe.wait_ge(s[l]["x_mixed"], m - 3)
                    for k in range(KT):
                        last = mm(bank[m % 4][:, 0:T], wout[:, m, k, :], hT[:, k, :], k == 0, k == KT - 1)
                    last.then_inc(s[l]["y_ps"], 1)
                    if m >= 2:
                        squares(2 * l + 1, m - 2)
                for k in range(KT - 2, KT):
                    squares(2 * l + 1, k)

            def queries(l):
                def sub_scores(h):
                    pe.wait_ge(s[l]["q_copied"], 2 * h + 2)
                    pe.wait_ge(keys_in, 16 * (l + 1))
                    if h >= 2:
                        pe.wait_ge(s[l]["key_copied"], h - 1)
                    for side in range(2):
                        for t in range(TT):
                            c = (side * TT + t) * NKEY
                            last = mm(bank[4 + h % 2][:, c:c + NKEY], qs[:, h % 2, side, t * P:(t + 1) * P], keys[:, h, side, :])
                    last.then_inc(s[l]["key_ps"], 1)

                for h in range(PH):
                    pe.wait_ge(wq_in[h % WQ_RING], 16 * (PH // WQ_RING * l + h // WQ_RING + 1))
                    for side in range(2):
                        u = 2 * h + side
                        if u >= 4:
                            pe.wait_ge(s[l]["q_copied"], u - 3)
                        for k in range(KT):
                            if u == 0:
                                pe.wait_ge(norms["h_ready"], KT * (2 * l + 1) + k + 1)
                            last = mm(bank[u % 4][:, 0:T], wq[:, h % WQ_RING, side, k, :], hT[:, k, :], k == 0, k == KT - 1)
                        last.then_inc(s[l]["q_ps"], 1)
                    if h:
                        sub_scores(h - 1)
                sub_scores(PH - 1)
                for n in range(4):
                    t, side = n // 2, n % 2
                    pe.wait_ge(s[l]["sel_ready"], n + 1)
                    c = side * T + t * P
                    for k in range(TOPK):
                        mm(bank[6][:, c:c + P], q_hot[n].rearrange("p h k a -> p (h k) a")[:, :, k], ident, k == 0, k == TOPK - 1)
                pe.wait_ge(s[l]["pick_ready"], 1)
                for t in range(TT):
                    last = nc.tensor.transpose(bank[7][:, t * P:(t + 1) * P], q_g[:, t].rearrange("p h k -> p (h k)"), ident)
                last.then_inc(s[l]["pick_ps"], 1)

            def dense_gates(l):
                def group(g, r, wait):
                    if wait:
                        pe.wait_ge(s[l]["g_copied"], g - 3)
                    pe.wait_ge(s[l]["hot_first"], g + 1)
                    pe.wait_ge(s[l]["hot_gate"], g + 1)
                    for n in range(4):
                        last = mm(bank[r][:, n * P:(n + 1) * P], hot[r][:, 0, n, :], hot[r][:, 1, n, :])
                    last.then_inc(s[l]["hot_used"], 1)

                for r in range(4):
                    group(r, r, False)
                with pe.Fori(1, T // 16) as i:
                    for r in range(4):
                        group(4 * i + r, r, True)

            def experts(l):
                def up(j, r, wait):
                    if wait:
                        pe.wait_ge(s[l]["s_gelu"], j - 1)
                    o = bank[4 + r][:, 0:T]
                    for h in range(2):
                        pe.wait_ge(s[l]["uh_done"], 2 * j + h + 1)
                        pe.wait_ge(s[l]["ul_done"], 2 * j + h + 1)
                        for k in range(h * KT // 2, (h + 1) * KT // 2):
                            c = slice(k * P, (k + 1) * P)
                            mm(o, u_hi[:, c], x_hi[:, k, :], k == 0, False)
                            mm(o, u_hi[:, c], x_lo[:, k, :], False, False)
                            last = mm(o, u_lo[:, c], x_hi[:, k, :], False, k == KT - 1)
                        last.then_inc(s[l]["u_used"], 1)

                def down(j, r, first=False, end=False):
                    pe.wait_ge(s[l]["ah_done"], j + 1)
                    pe.wait_ge(s[l]["al_done"], j + 1)
                    for h in range(2):
                        pe.wait_ge(s[l]["vh_done"], 2 * j + h + 1)
                        pe.wait_ge(s[l]["vl_done"], 2 * j + h + 1)
                        c = slice(h * HALF, (h + 1) * HALF)
                        for t in range(TT):
                            o, tok = bank[2 * t + h][:, :], slice(t * P, (t + 1) * P)
                            mm(o, a_hi[:, r, tok], v_hi[:, c], first, False, True)
                            mm(o, a_hi[:, r, tok], v_lo[:, c], False, False, True)
                            last = mm(o, a_lo[:, r, tok], v_hi[:, c], False, end, True)
                        last.then_inc(s[l]["v_used"], 1)

                pe.wait_ge(s[l]["xh_done"], 1)
                pe.wait_ge(s[l]["xl_done"], 1)
                up(0, 0, False)
                up(1, 1, False)
                down(0, 0, first=True)
                with pe.Fori(1, NKEY // 2) as i:
                    for r in range(2):
                        up(2 * i + r, r, True)
                        down(2 * i + r - 1, 1 - r)
                down(NKEY - 1, 1, end=True)

            def expert_out(l):
                pe.wait_ge(s[l]["e_copied"], 4)
                for m in range(KT):
                    for t in range(TT):
                        c = (m % 2) * T + t * P
                        last = nc.tensor.transpose(bank[4 + m // 2][:, c:c + P], yt[:, t, m * P:(m + 1) * P], ident)
                    if m % 2:
                        last.then_inc(s[l]["eT_ps"], 1)

            pe.wait_ge(const_in, 48)
            for l in range(LAYERS):
                for k in range(KT):
                    squares(2 * l, k)
                project(l)
                attend(l)
                if l == 0:
                    pe.wait_ge(s[0]["sub_sq"], 1)
                    for n in range(2):
                        last = mm(bank[n][:, :], ones, big[:, n * 512:(n + 1) * 512])
                    last.then_inc(s[0]["sub_ps"], 1)
                mixer_out(l)
                queries(l)
                dense_gates(l)
                experts(l)
                expert_out(l)
            for k in range(KT):
                squares(4, k)

        @block.scalar
        def _(act):
            steps = [0]

            def link(ins):
                steps[0] += 1
                ins.then_inc(act_step, 1)
                act.wait_ge(act_step, steps[0])

            f = nc.scalar.activation

            def norm(i):
                for k in range(KT):
                    if i:
                        act.wait_ge(s[(i - 1) // 2]["x_mixed" if i % 2 else "x_done"], k + 1)
                    if i or k >= 4:
                        act.wait_ge(norms["ss_ps"], KT * i + k - 3 if k >= 4 else KT * i)
                    f(work[:, k % 4, :], xT[:, k, :], ACT.Square).then_inc(norms["sq_ready"], 1)
                act.wait_ge(norms["rec_ready"], i + 1)
                f(work[:, 1, :], work[:, 0, :], ACT.Sqrt).then_inc(norms["root_ready"], 1)
                for k in range(KT):
                    act.wait_ge(norms["hat_ready"], KT * i + k + 1)
                    if i < 4:
                        shift = mod[i // 2][:, 3 * (i % 2) * KT + k:3 * (i % 2) * KT + k + 1]
                        f(hT[:, k, :], hT[:, k, :], ACT.Identity, bias=shift).then_inc(norms["h_ready"], 1)

            def project(l):
                for u in range(0, QK_UNITS[l], 2):
                    act.wait_ge(s[l]["qk_ps"], u + 1)
                    n = u - QK_TILES[l]
                    if n < 0:
                        ins = f(qk[:, u, :], bank[u % 4][:, 0:T], ACT.Copy, scale=HD ** -0.5 if u in Q_TILES[l] else 1.0)
                    elif n < 2 * TT:
                        part, t = n // TT, n % TT
                        w = V_WIDTHS[l][part]
                        ins = f(vv[:, t, part * 512:part * 512 + w], bank[u % 4][:, 0:w], ACT.Copy)
                    else:
                        link(f(softp, bank[u % 4][0:8, 0:T], ACT.Abs, bias=f_bias))
                        link(f(softp, softp, ACT.Exp, scale=-1.0))
                        ins = f(softp, softp, ACT.Ln, bias=1.0)
                    ins.then_inc(s[l]["qk_act"], 1)

            def exps(l, g):
                act.wait_ge(s[l]["neg_ready"], g + 1)
                for i in range(4 * g, 4 * g + 4):
                    for t in range(TT):
                        c = scores[:, i, P * t:P * t + P * (t + 1)]
                        last = f(c, c, ACT.Exp, bias=neg[:, 2 * i + t:2 * i + t + 1], accum_out=den[:, 2 * i + t:2 * i + t + 1])
                if l == 1 and g < 2:
                    c = snk[:, 8 * g:8 * g + 8]
                    last = f(c, c, ACT.Exp)
                last.then_inc(s[l]["exp_done"], 1)

            def attend(l):
                prods = value_products(l)
                done = 0
                for g in range(6):
                    if g < 4:
                        exps(l, g)
                    if g >= 2:
                        ready = len([1 for v in prods if v[0] < 4 * (g - 1)])
                        for n in range(done, ready):
                            act.wait_ge(s[l]["pt_ps"], n + 1)
                            if n >= 4:
                                act.wait_ge(s[l]["av_ps"], prods[n - 4][3] + 1)
                            f(pT[:, n % 4, :], bank[4 + n % 2][:, 0:MAPW], ACT.Copy).then_inc(s[l]["pt_copied"], 1)
                        done = ready

            for l in range(LAYERS):
                if l == 0:
                    act.wait_ge(c_in, 16)
                    f(work[:].rearrange("p a b -> p (a b)"), c_all[:], ACT.Exp, scale=-1.0).then_inc(silu_e, 1)
                    act.wait_ge(const_in, 48)
                    act.wait_ge(lam_s, 1)
                    f(lam[:, 2:4], lam[:, 0:2], ACT.Exp).then_inc(lam_e, 1)
                norm(2 * l)
                project(l)
                attend(l)
                if l == 0:
                    act.wait_ge(s[0]["av_copied"], KT)
                    f(big[:, 0:1024], hT[:, 4:8, :].rearrange("p k t -> p (k t)"), ACT.Square).then_inc(s[0]["sub_sq"], 1)
                    act.wait_ge(s[0]["sub_rec"], 1)
                    f(big[:, 1024:2048], big[:, 0:1024], ACT.Sqrt).then_inc(s[0]["sub_root"], 1)
                norm(2 * l + 1)
                act.wait_ge(norms["h_ready"], KT * (2 * l + 2))
                f(x_hi[:], hT[:], ACT.Copy).then_inc(s[l]["xh_done"], 1)
                def copy_keys(h):
                    act.wait_ge(s[l]["key_ps"], h + 1)
                    if h >= 2:
                        act.wait_ge(s[l]["key_free"], h - 1)
                    f(q_key[:, h % 2].rearrange("p s t n -> p (s t n)"), bank[4 + h % 2][:, :], ACT.Copy).then_inc(s[l]["key_copied"], 1)

                for h in range(PH):
                    for side in range(2):
                        u = 2 * h + side
                        act.wait_ge(s[l]["q_ps"], u + 1)
                        if h >= 2:
                            act.wait_ge(s[l]["key_ps"], h - 1)
                        f(qs[:, h % 2, side, :], bank[u % 4][:, 0:T], ACT.Copy).then_inc(s[l]["q_copied"], 1)
                    if h:
                        copy_keys(h - 1)
                copy_keys(PH - 1)
                act.wait_ge(s[l]["gate_max"], 1)
                f(q_e[:], q_e[:], ACT.Exp).then_inc(s[l]["gate_exp"], 1)

                act.wait_ge(s[l]["pick_copied"], 2)

                def copy_gates(g, r):
                    act.wait_ge(s[l]["hot_used"], g + 1)
                    dst = gates[:, :, bass.ds(4 * g, 4)]
                    f(dst, bank[r][:, :].rearrange("p (t j) -> p j t", t=4), ACT.Copy).then_inc(s[l]["g_copied"], 1)

                with act.Fori(0, T // 16) as i:
                    for r in range(4):
                        copy_gates(4 * i + r, r)

                def split_u(j, r, h, round_, wait):
                    act.wait_ge(u_in[r], 16 * (round_ + 1) + 16 * l * (NKEY // RINGS))
                    if wait:
                        act.wait_ge(s[l]["u_used"], 2 * j + h - 1)
                    c = slice(h * HALF, (h + 1) * HALF)
                    f(u_hi[:, c], raw[:, r, c], ACT.Copy).then_inc(s[l]["uh_done"], 1)

                def step(j, r, round_, wait=True, more=True, first=False):
                    if more:
                        split_u(j + 1, 1 - r, 0, round_ + r, True)
                    act.wait_ge(s[l]["u_used"], 2 * j + 2)
                    if wait:
                        act.wait_ge(s[l]["al_done"], j - 1)
                    f(work[:, r, :], bank[4 + r][:, 0:T], ACT.Gelu).then_inc(s[l]["s_gelu"], 1)
                    if more:
                        split_u(j + 1, 1 - r, 1, round_ + r, True)
                    act.wait_ge(s[l]["a_ready"], j + 1)
                    if wait:
                        act.wait_ge(s[l]["v_used"], 2 * j - 2)
                    f(a_hi[:, r, :], work[:, r, :], ACT.Copy).then_inc(s[l]["ah_done"], 1)
                    act.wait_ge(v_in[r], 16 * (round_ + 1) + 16 * l * (NKEY // RINGS))
                    for h in range(2):
                        if not first:
                            act.wait_ge(s[l]["v_used"], 2 * j + h - 1)
                        c = slice(h * HALF, (h + 1) * HALF)
                        f(v_hi[:, c], raw[:, RINGS + r, c], ACT.Copy).then_inc(s[l]["vh_done"], 1)

                for h in range(2):
                    split_u(0, 0, h, 0, False)
                step(0, 0, 0, wait=False, first=True)
                step(1, 1, 0, wait=False)
                with act.Fori(1, NKEY // 2 - 1) as i:
                    for r in range(2):
                        step(2 * i + r, r, i)
                step(NKEY - 2, 0, NKEY // 2 - 1)
                step(NKEY - 1, 1, NKEY // 2 - 1, more=False)
                for n in range(0, 4, 2):
                    act.wait_ge(s[l]["v_used"], 2 * NKEY)
                    f(yt[:, n // 2, 0:512], bank[n][:, :], ACT.Copy).then_inc(s[l]["e_copied"], 1)
            norm(4)

        @block.vector
        def _(dve):
            steps = [0]

            def link(ins):
                steps[0] += 1
                ins.then_inc(dve_step, 1)
                dve.wait_ge(dve_step, steps[0])

            v = nc.vector

            def root(y, m, t):
                link(v.scalar_tensor_tensor(out=t, in0=y, scalar=-0.5, in1=y, op0=ALU.mult, op1=ALU.mult))
                link(v.tensor_tensor(t, t, m, ALU.mult))
                link(v.scalar_tensor_tensor(out=y, in0=t, scalar=1.5, in1=y, op0=ALU.add, op1=ALU.mult))

            def norm_root(i):
                dve.wait_ge(norms["ss_ps"], KT * (i + 1))
                link(v.tensor_scalar(work[:, 2, :], bank[7 if i % 2 else 0][:, 0:T], 1.0 / D, EPS, ALU.mult, ALU.add))
                v.reciprocal(work[:, 0, :], work[:, 2, :]).then_inc(norms["rec_ready"], 1)
                dve.wait_ge(norms["root_ready"], i + 1)
                root(work[:, 1, :], work[:, 2, :], work[:, 3, :])

            def norm_scale(i):
                for k in range(KT):
                    g = gain(4) if i == 4 else amp[i // 2][i % 2]
                    v.scalar_tensor_tensor(out=hT[:, k, :], in0=xT[:, k, :], scalar=g[:, k:k + 1], in1=work[:, 1, :],
                                           op0=ALU.mult, op1=ALU.mult).then_inc(norms["hat_ready"], 1)

            def modulate(l, lo, hi):
                for n in range(lo, hi):
                    r = n % MODS
                    dve.wait_ge(wm_in[r], 16 * (n // MODS + 1))
                    v.tensor_tensor_reduce(wmod_ring[:, r, :], wmod_ring[:, r, :], c_all[:], 1.0, 0.0, ALU.mult, ALU.add,
                                           mod[l][:, n:n + 1]).then_inc(s[l]["mod_tile"], 1)

            def finish_modulation(l, lo, hi, norms):
                dve.wait_ge(s[l]["mod_tile"], hi)
                link(v.tensor_tensor(mod[l][:, lo:hi], mod[l][:, lo:hi], b_mod(l)[:, lo:hi], ALU.add))
                for n in norms:
                    link(v.scalar_tensor_tensor(out=amp[l][n], in0=mod[l][:, (3 * n + 1) * KT:(3 * n + 2) * KT], scalar=1.0,
                                                in1=gain(2 * n + l), op0=ALU.add, op1=ALU.mult))

            def project(l):
                for u in range(1, QK_UNITS[l], 2):
                    dve.wait_ge(s[l]["qk_ps"], u + 1)
                    n = u - QK_TILES[l]
                    if n < 0:
                        ins = v.tensor_scalar(qk[:, u, :], bank[u % 4][:, 0:T], HD ** -0.5 if u in Q_TILES[l] else 1.0, None, ALU.mult)
                    else:
                        part, t = n // TT, n % TT
                        w = V_WIDTHS[l][part]
                        ins = v.tensor_copy(vv[:, t, part * 512:part * 512 + w], bank[u % 4][:, 0:w])
                    ins.then_inc(s[l]["qk_dve"], 1)
                    if l == 0:
                        rest, units, n = NMOD - EARLY, unit_counts(0)[1] - 1, u // 2 - 1
                        if n >= 0:
                            modulate(0, EARLY + rest * n // units, EARLY + rest * (n + 1) // units)
                if l == 0:
                    dve.wait_ge(s[l]["qk_act"], unit_counts(l)[0])
                    link(v.tensor_scalar(minz, bank[(QK_UNITS[l] - 1) % 4][0:8, 0:T], f_bias, 0.0, ALU.add, ALU.min))
                    v.tensor_tensor_scan(cum, minz, softp, 0.0, ALU.add, ALU.subtract).then_inc(s[l]["cum_ready"], 1)
                    dve.wait_ge(s[l]["cum_ready"], 1)
                    v.tensor_scalar(negcum, cum, -1.0, None, ALU.mult).then_inc(s[l]["cum_ready"], 1)

            def maxima(l, g):
                for i in range(4 * g, 4 * g + 4):
                    b = bias_map(l, attention_maps(l)[i][3])
                    dve.wait_ge(s[l]["map_ps"], i + 1)
                    for t in range(TT):
                        c = slice(P * t, P * t + P * (t + 1))
                        v.tensor_tensor_reduce(scores[:, i, c], bank[i % 4][:, c], b[:, c], 1.0, -3e38, ALU.add, ALU.max,
                                               mx[:, 2 * i + t:2 * i + t + 1]).then_inc(s[l]["map_max"], 1)
                dve.wait_ge(s[l]["map_max"], 8 * (g + 1))
                c = slice(8 * g, 8 * g + 8)
                if l == 1 and g < 2:
                    sk = sinks[:, 4 * g:4 * g + 4].unsqueeze(2).to_broadcast([P, 4, 2])
                    link(v.tensor_tensor(mx[:, c].rearrange("p (a b) -> p a b", b=2), mx[:, c].rearrange("p (a b) -> p a b", b=2), sk, ALU.max))
                    link(v.tensor_tensor(snk[:, c].rearrange("p (a b) -> p a b", b=2), sk, mx[:, c].rearrange("p (a b) -> p a b", b=2), ALU.subtract))
                v.tensor_scalar(neg[:, c], mx[:, c], -1.0, None, ALU.mult).then_inc(s[l]["neg_ready"], 1)

            def normalise(l, g):
                dve.wait_ge(s[l]["exp_done"], g + 1)
                c = slice(8 * g, 8 * g + 8)
                if l == 1 and g < 2:
                    link(v.tensor_tensor(den[:, c], den[:, c], snk[:, c], ALU.add))
                link(v.reciprocal(rec[:, c], den[:, c]))
                if l == 0 and g >= 2:
                    m1 = rec[:, c].rearrange("p (h m t) -> p h m t", h=2, m=2)[:, :, 1, :]
                    link(v.tensor_scalar(m1, m1, lam[:, 7:8], None, ALU.mult))
                    for i in (4 * g, 4 * g + 2):
                        for t in range(TT):
                            cc = slice(P * t, P * t + P * (t + 1))
                            r0 = rec[:, 2 * i + t:2 * i + t + 1]
                            r1 = rec[:, 2 * i + 2 + t:2 * i + 3 + t]
                            link(v.tensor_scalar(scores[:, i, cc], scores[:, i, cc], r0, None, ALU.mult))
                            last = v.scalar_tensor_tensor(out=scores[:, i, cc], in0=scores[:, i + 1, cc], scalar=r1,
                                                          in1=scores[:, i, cc], op0=ALU.mult, op1=ALU.add)
                else:
                    for i in range(4 * g, 4 * g + 4):
                        for t in range(TT):
                            cc = slice(P * t, P * t + P * (t + 1))
                            last = v.tensor_scalar(scores[:, i, cc], scores[:, i, cc], rec[:, 2 * i + t:2 * i + t + 1], None, ALU.mult)
                last.then_inc(s[l]["prob_ready"], 1)

            def heads_out(l, g):
                lo, hi = [len({p[3] for p in value_products(l) if p[0] < 4 * n}) for n in (g, g + 1)]
                for tile in range(lo, hi):
                    dve.wait_ge(s[l]["av_ps"], tile + 1)
                    v.tensor_copy(hT[:, tile, :], bank[6 + tile % 2][:, 0:T]).then_inc(s[l]["av_copied"], 1)

            def attend(l):
                dve.wait_ge(bias_in, 16 * (l + 1))
                maxima(l, 0)
                maxima(l, 1)
                normalise(l, 0)
                maxima(l, 2)
                normalise(l, 1)
                heads_out(l, 0)
                maxima(l, 3)
                normalise(l, 2)
                heads_out(l, 1)
                normalise(l, 3)
                heads_out(l, 2)
                heads_out(l, 3)

            def sub_norm():
                dve.wait_ge(s[0]["sub_ps"], 1)
                m, r, y, t = (big[:, 2048:3072], big[:, 0:1024], big[:, 1024:2048], big[:, 3072:4096])
                for n in range(2):
                    last = v.tensor_scalar(m[:, n * 512:(n + 1) * 512], bank[n][:, :], 1.0 / P, EPS, ALU.mult, ALU.add)
                link(last)
                v.reciprocal(r, m).then_inc(s[0]["sub_rec"], 1)
                dve.wait_ge(s[0]["sub_root"], 1)
                root(y, m, t)
                o = hT[:, 4:8, :].rearrange("p k t -> p (k t)")
                v.scalar_tensor_tensor(out=o, in0=o, scalar=subln_s, in1=y, op0=ALU.mult, op1=ALU.mult).then_inc(s[0]["mix_ready"], 1)

            def top16(pairs):
                for src, _, val, _ in pairs:
                    ins = v.max(val[:, 0:8], src)
                link(ins)
                for src, rep, val, idx in pairs:
                    v.max_index(idx[:, 0:8], val[:, 0:8], src)
                    ins = v.match_replace(rep, val[:, 0:8], src, -3e38)
                link(ins)
                for _, rep, val, _ in pairs:
                    ins = v.max(val[:, 8:16], rep)
                link(ins)
                for _, rep, val, idx in pairs:
                    ins = v.max_index(idx[:, 8:16], val[:, 8:16], rep)
                return ins

            def retrieve(l):
                for h in range(PH):
                    dve.wait_ge(s[l]["key_copied"], h + 1)
                    ins = top16([(q_key[:, h % 2, side, t, :], q_rep[:, side, t, :],
                                  q_val[:, t, h, side, :], q_idx[:, t, h, side, :]) for side in range(2) for t in range(TT)])
                    ins.then_inc(s[l]["key_free"], 1)
                    dve.wait_ge(s[l]["key_free"], h + 1)
                    edge = WIDE * TOPK
                    for lo, hi, n, area in ((0, WIDE, TOPK, q_cand[:, :, 0:edge]), (WIDE, TOPK, 4, q_cand[:, :, edge:NCAND])):
                        ins = v.tensor_tensor(area.rearrange("p t (a b) -> p t a b", b=n),
                                              q_val[:, :, h, 0, lo:hi].unsqueeze(3).to_broadcast([P, TT, hi - lo, n]),
                                              q_val[:, :, h, 1, 0:n].unsqueeze(2).to_broadcast([P, TT, hi - lo, n]), ALU.add)
                    link(ins)
                    link(top16([(q_cand[:, t, :], q_rep2[:, t, :], q_top[:, t, h, :], q_pos[:, t, h, :])
                                for t in range(TT)]))
                v.tensor_tensor(q_e[:], q_top[:], q_top[:, :, :, 0:1].to_broadcast([P, TT, PH, TOPK]), ALU.subtract)\
                    .then_inc(s[l]["gate_max"], 1)
                pos = q_pos[:].rearrange("p t h k -> p (t h k)")
                far, d1, d2 = q_tmp
                v.tensor_single_scalar(q_ab[0], pos, 4, ALU.logical_shift_right)
                v.tensor_single_scalar(q_ab[1], pos, 15, ALU.bitwise_and)
                v.tensor_single_scalar(q_ab[2], pos, 2, ALU.logical_shift_right)
                v.tensor_single_scalar(q_ab[3], pos, 3, ALU.bitwise_and)
                link(v.tensor_scalar(far, pos, float(WIDE * TOPK), None, ALU.is_ge))
                v.tensor_tensor(d1, q_ab[2], q_ab[0], ALU.subtract)
                link(v.tensor_tensor(d2, q_ab[3], q_ab[1], ALU.subtract))
                v.scalar_tensor_tensor(out=d1, in0=d1, scalar=float(WIDE - WIDE * TOPK // 4), in1=far, op0=ALU.add, op1=ALU.mult)
                link(v.tensor_tensor(d2, d2, far, ALU.mult))
                for n, d in ((0, d1), (1, d2)):
                    v.tensor_tensor(q_abf[n][:].rearrange("p t n -> p (t n)"), d, q_ab[n], ALU.add)
                link(v.tensor_copy(q_idf[:], q_idx[:]))
                for n in range(4):
                    v.tensor_tensor(q_hot[n].rearrange("p h k a -> p (h k) a"), q_abf[n % 2][:, n // 2, :].unsqueeze(2).to_broadcast([P, P, TOPK]),
                                    iota[:, 0:TOPK].unsqueeze(1).to_broadcast([P, P, TOPK]), ALU.is_equal).then_inc(s[l]["equal_ready"], 1)
                dve.wait_ge(s[l]["gate_exp"], 1)
                link(v.reduce_sum(gsum.rearrange("p (t h) -> p t h", t=TT), q_e[:], axis=AX_X))
                link(v.reciprocal(grec, gsum))
                v.tensor_tensor(q_g[:], q_e[:], grec.rearrange("p (t h) -> p t h", t=TT).unsqueeze(3).to_broadcast([P, TT, PH, TOPK]), ALU.mult)\
                    .then_inc(s[l]["pick_ready"], 1)
                v.tensor_copy(iota_bf, iota.unsqueeze(2).to_broadcast([P, P, 4]))
                dve.wait_ge(s[l]["pick_ps"], 1)
                v.tensor_copy(pick[:, 0:2, :].rearrange("p a b -> p (a b)"), bank[6][:, :]).then_inc(s[l]["pick_copied"], 1)
                v.tensor_copy(pick[:, 2, :], bank[7][:, 0:T]).then_inc(s[l]["pick_copied"], 1)

            def one_hots(l):
                dve.wait_ge(s[l]["pick_copied"], 2)
                link(v.tensor_copy(pick_bf, pick[:, 1, :]))

                def group(g, r, wait):
                    if wait:
                        dve.wait_ge(s[l]["hot_used"], g - 3)
                    if wait or r >= 2:
                        dve.wait_ge(s[l]["hot_gate"], g - 1)
                    v.tensor_tensor(hot_bf[r % 2], iota_bf, pick_bf[:, bass.ds(4 * g, 4)].unsqueeze(1).to_broadcast([P, P, 4]), ALU.is_equal)\
                        .then_inc(s[l]["hot_second"], 1)
                    v.tensor_tensor(hot[r][:, 0], iota.unsqueeze(1).to_broadcast([P, 4, P]),
                                    pick[:, 0, bass.ds(4 * g, 4)].unsqueeze(2).to_broadcast([P, 4, P]), ALU.is_equal)\
                        .then_inc(s[l]["hot_first"], 1)

                for r in range(4):
                    group(r, r, False)
                with dve.Fori(1, T // 16) as i:
                    for r in range(4):
                        group(4 * i + r, r, True)

            def experts(l):
                dve.wait_ge(s[l]["g_copied"], T // 4)

                def lower_u(j, r, h):
                    dve.wait_ge(s[l]["uh_done"], 2 * j + h + 1)
                    c = slice(h * HALF, (h + 1) * HALF)
                    v.tensor_tensor(u_lo[:, c], raw[:, r, c], u_hi[:, c].bitcast(F32), ALU.subtract).then_inc(s[l]["ul_done"], 1)

                def step(j, r, more=True):
                    if more:
                        lower_u(j + 1, 1 - r, 0)
                    dve.wait_ge(s[l]["s_gelu"], j + 1)
                    v.tensor_tensor(work[:, r, :], work[:, r, :], gates[:, bass.ds(j, 1), :].rearrange("p a t -> p (a t)"), ALU.mult)\
                        .then_inc(s[l]["a_ready"], 1)
                    if more:
                        lower_u(j + 1, 1 - r, 1)
                    dve.wait_ge(s[l]["ah_done"], j + 1)
                    v.tensor_tensor(a_lo[:, r, :], work[:, r, :], a_hi[:, r, :].bitcast(F32), ALU.subtract).then_inc(s[l]["al_done"], 1)
                    for h in range(2):
                        dve.wait_ge(s[l]["vh_done"], 2 * j + h + 1)
                        c = slice(h * HALF, (h + 1) * HALF)
                        v.tensor_tensor(v_lo[:, c], raw[:, RINGS + r, c], v_hi[:, c].bitcast(F32), ALU.subtract).then_inc(s[l]["vl_done"], 1)

                def next_modulation(n, r, i):
                    dve.wait_ge(wm1_in[r], 16 * (i + 1))
                    v.tensor_tensor_reduce(wmod_ring[:, r, :], wmod_ring[:, r, :], c_all[:], 1.0, 0.0, ALU.mult, ALU.add,
                                           tile_sum[:, r:r + 1]).then_inc(s[1]["mod_tile"], 1)
                    dve.wait_ge(s[1]["mod_tile"], n + 1)
                    v.tensor_copy(mod[1][:, bass.ds(n, 1)], tile_sum[:, r:r + 1]).then_inc(s[1]["mod_kept"], 1)

                for h in range(2):
                    lower_u(0, 0, h)
                step(0, 0)
                step(1, 1)
                if l == 0:
                    with dve.Fori(1, 1 + NMOD // 2) as i:
                        for r in range(2):
                            step(2 * i + r, r)
                            next_modulation(2 * i - 2 + r, r, i - 1)
                with dve.Fori(1 + (NMOD // 2 if l == 0 else 0), NKEY // 2 - 1) as i:
                    for r in range(2):
                        step(2 * i + r, r)
                step(NKEY - 2, 0)
                step(NKEY - 1, 1, more=False)

            dve.wait_ge(silu_e, 1)
            cw = work[:].rearrange("p a b -> p (a b)")
            link(v.tensor_scalar(cw, cw, 1.0, None, ALU.add))
            link(v.reciprocal(cw, cw))
            link(v.tensor_tensor(c_all[:], c_all[:], cw, ALU.mult))
            dve.wait_ge(const_in, 48)
            for n in range(2):
                ins = v.tensor_tensor_reduce(stat[:, n * HD:(n + 1) * HD], lam_in[:, 2 * n, :], lam_in[:, 2 * n + 1, :], 1.0, 0.0,
                                             ALU.mult, ALU.add, lam[:, n:n + 1])
            ins.then_inc(lam_s, 1)
            dve.wait_ge(lam_e, 1)
            link(v.tensor_tensor(lam[:, 6:7], lam[:, 3:4], lam[:, 2:3], ALU.subtract))
            v.tensor_scalar(lam[:, 7:8], lam[:, 6:7], -LAM_INIT, None, ALU.add)
            link(v.tensor_scalar(subln_s, subln, 1.0 - LAM_INIT, None, ALU.mult))

            for l in range(LAYERS):
                norm_root(2 * l)
                if l == 0:
                    modulate(0, 0, EARLY)
                    finish_modulation(0, 0, EARLY, (0,))
                norm_scale(2 * l)
                project(l)
                if l == 0:
                    finish_modulation(0, EARLY, NMOD, (1,))
                attend(l)
                if l == 0:
                    sub_norm()
                for m in range(KT):
                    dve.wait_ge(s[l]["y_ps"], m + 1)
                    v.scalar_tensor_tensor(out=xT[:, m, :], in0=bank[m % 4][:, 0:T], scalar=mod[l][:, 2 * KT + m:2 * KT + m + 1],
                                           in1=xT[:, m, :], op0=ALU.mult, op1=ALU.add).then_inc(s[l]["x_mixed"], 1)
                norm_root(2 * l + 1)
                norm_scale(2 * l + 1)
                dve.wait_ge(s[l]["xh_done"], 1)
                v.tensor_tensor(x_lo[:], hT[:], x_hi[:].bitcast(F32), ALU.subtract).then_inc(s[l]["xl_done"], 1)
                retrieve(l)
                one_hots(l)
                experts(l)
                if l == 0:
                    dve.wait_ge(s[1]["mod_kept"], NMOD)
                    finish_modulation(1, 0, NMOD, (0, 1))
                for n in range(1, 4, 2):
                    dve.wait_ge(s[l]["v_used"], 2 * NKEY)
                    v.tensor_copy(yt[:, n // 2, 512:1024], bank[n][:, :]).then_inc(s[l]["e_copied"], 1)
                dve.wait_ge(x_back, 16 * (l + 1))
                for m in range(KT):
                    dve.wait_ge(s[l]["eT_ps"], m // 2 + 1)
                    c = (m % 2) * T
                    v.scalar_tensor_tensor(out=xT[:, m, :], in0=bank[4 + m // 2][:, c:c + T], scalar=mod[l][:, 5 * KT + m:5 * KT + m + 1],
                                           in1=xT[:, m, :], op0=ALU.mult, op1=ALU.add).then_inc(s[l]["x_done"], 1)
            norm_root(4)
            norm_scale(4)


def t5_bucket(rel):
    n = np.abs(rel)
    nf = np.maximum(n, 1).astype(np.float32)
    large = 8 + (np.log(nf / np.float32(8)) / np.float32(math.log(512 / 8)) * np.float32(8)).astype(np.int32)
    return np.where(rel > 0, 16, 0) + np.where(n < 8, n, np.minimum(large, 15))


def map_layout(full, seen):
    full = np.where(seen, full, np.float32(NEG))
    return np.concatenate([full[:P, :P], full[P:, :]], axis=1)


def tiles_of(w, cols):
    return w[:, cols].reshape(KT, P, len(cols) // P, P).transpose(1, 2, 0, 3).reshape(P, -1)


def moving_of(w, cols):
    return w[:, cols].reshape(KT, P, len(cols)).transpose(1, 0, 2).reshape(P, -1)


def by_partition(v):
    return v.reshape(-1, P).T


def kernel(**inputs):
    import concourse.bacc as bacc
    from concourse.bass_utils import run_bass_kernel_spmd

    i = {k: np.asarray(v) for k, v in inputs.items()}
    r = np.arange
    q, k = r(T)[:, None], r(T)[None, :]
    qc, kc = q // CHUNK, k // CHUNK
    arrays = {}
    arrays["x"] = i["x"][0].T.reshape(KT, P, T).transpose(1, 0, 2).reshape(P, -1)
    consts = np.zeros((P, C_END), np.float32)
    consts[:, C_ID:C_ID + P] = np.eye(P)
    consts[:, C_ONE:C_ONE + P] = 1.0
    consts[:, C_IOTA:C_IOTA + P] = r(P)
    arrays["consts"] = consts
    par = np.zeros((P, 408), np.float32)
    for l in range(LAYERS):
        par[:, l * NMOD:(l + 1) * NMOD] = by_partition(i["b_mod"][l])
        par[:, 96 + l * KT:96 + (l + 1) * KT] = by_partition(i["norm_mix"][l])
        par[:, 112 + l * KT:112 + (l + 1) * KT] = by_partition(i["norm_ffn"][l])
    par[:, 128:136] = by_partition(i["final_norm"])
    par[0:8, 136] = i["fox_f_bias"][0]
    par[:, 137] = i["diff_subln"][0]
    order = [m // 2 + 4 * (m % 2) for m in range(8)]
    par[:, 144:152] = i["swa_sinks"][0][order]
    par[:, 152:408] = i["diff_lambda"][0].reshape(1, -1)
    arrays["params"] = par
    arrays["c"] = i["c"]
    arrays["w_mod"] = i["w_mod"].transpose(0, 2, 1).reshape(LAYERS, NMOD, P, D)
    w = i["even_w_in"][0]
    arrays["w_in0"] = np.concatenate([
        tiles_of(w, np.concatenate([r(0, 1024), r(1544, 2568)])),
        moving_of(w, r(1024, 1536)), moving_of(w, r(2568, 3080)), moving_of(w, r(1536, 1544))], axis=1)
    w = i["odd_w_in"][0]
    heads = np.concatenate([r(h * HD, (h + 1) * HD) for h in order])
    arrays["w_in1"] = np.concatenate([
        tiles_of(w, np.concatenate([heads, r(512, 640), r(768, 1280), r(1280, 1792)])),
        moving_of(w, r(1792, 2304)), moving_of(w, r(640, 768))], axis=1)
    rows = np.concatenate([heads, r(512, 1024)])
    arrays["w_out"] = np.stack([tiles_of(i["even_w_out"][0], r(D)), tiles_of(i["odd_w_out"][0][rows], r(D))])
    t5 = i["t5_bias"][t5_bucket(k - q)]
    causal, chunked = k <= q, kc <= qc
    windowed = chunked & (kc >= qc - 1)
    arrays["bias0"] = np.concatenate([map_layout(np.zeros((T, T), np.float32), causal)]
                                     + [map_layout(t5[:, :, h], chunked) for h in range(4)], axis=1)
    rel = i["chunk_rel_bias"][0][q - k + 256]
    arrays["bias1"] = np.concatenate([map_layout(t5[:, :, h], windowed) for h in order]
                                     + [map_layout(rel[:, :, h], chunked) for h in range(8)], axis=1)
    arrays["w_q"] = np.stack([tiles_of(i["peer_w_q"][l], r(2 * D)) for l in range(LAYERS)])
    arrays["keys"] = i["peer_sub_keys"].transpose(0, 4, 1, 2, 3).reshape(LAYERS, P, -1)
    arrays["u"] = i["peer_u"].reshape(LAYERS, NKEY, NKEY, KT, P).transpose(0, 2, 4, 3, 1).reshape(LAYERS, NKEY, P, D)
    arrays["v"] = i["peer_v"].reshape(LAYERS, NKEY, NKEY, D).transpose(0, 2, 1, 3)

    nc = bacc.Bacc("TRN2", target_bir_lowering=False, num_devices=1)
    arrays = {f"in_{n}": np.ascontiguousarray(x) for n, x in arrays.items()}
    args = {n[3:]: nc.dram_tensor(n, x.shape, mybir.dt.from_np(x.dtype), kind="ExternalInput").ap() for n, x in arrays.items()}
    out = nc.dram_tensor("out_yT", (D, T), F32, kind="ExternalOutput").ap()
    build(nc, args, out)
    res = run_bass_kernel_spmd(nc, [arrays], core_ids=[0])
    return np.ascontiguousarray(np.asarray(res.results[0]["out_yT"]).T)[None]
```
